# Optimizing a Trainium2 kernel written in Bass

```python
import math
import jax, jax.numpy as jnp
from jax import lax
import numpy as np

D_MODEL = 2048
BATCH = 1
SEQ = 256
DEPTH = 1
DEC_BATCH = 1
DEC_SEQ = 32
PAST_LEN = 128

CHUNK = 64
WINDOW = 128
WINDOW_CHUNKS = WINDOW // CHUNK
HEAD_DIM = 64
N_HEADS = D_MODEL // HEAD_DIM
N_KV_HEADS = N_HEADS // 8
GROUP = N_HEADS // N_KV_HEADS
D_ATTN = N_HEADS * HEAD_DIM
D_KV = N_KV_HEADS * HEAD_DIM
D_CONV = D_MODEL
CONV_WIDTH = 3
D_FF = -(-8 * D_MODEL // (3 * 256)) * 256
ROPE_THETA = 10000.0
EPS = 1e-6
SCALE = HEAD_DIM ** -0.5
NEG_INF = -1e30
SPLITS = [D_ATTN, D_ATTN + D_KV, D_ATTN + 2 * D_KV,
          D_ATTN + 2 * D_KV + D_CONV, D_ATTN + 2 * D_KV + 2 * D_CONV,
          D_ATTN + 2 * D_KV + 3 * D_CONV, D_ATTN + 2 * D_KV + 3 * D_CONV + D_MODEL]
D_IN_PROJ = D_ATTN + 2 * D_KV + 3 * D_CONV + 2 * D_MODEL

kernel_name = 'hybrid_swa_sink_shortconv_stream_step'

def _rmsnorm(x, g):
    xf = x.astype(jnp.float32)
    y = xf * lax.rsqrt(jnp.mean(xf * xf, axis=-1, keepdims=True) + EPS)
    return (y * g.astype(jnp.float32)).astype(x.dtype)

def _rope(x, pos):
    half = HEAD_DIM // 2
    inv = jnp.exp(-math.log(ROPE_THETA) * jnp.arange(half, dtype=jnp.float32) * (2.0 / HEAD_DIM))
    ang = pos.astype(jnp.float32)[:, None] * inv[None, :]
    cos = jnp.cos(ang)[:, None, :]
    sin = jnp.sin(ang)[:, None, :]
    xf = x.astype(jnp.float32)
    x1, x2 = xf[..., :half], xf[..., half:]
    return jnp.concatenate([x1 * cos - x2 * sin, x2 * cos + x1 * sin], axis=-1).astype(x.dtype)

def _sink_softmax(s, sink):
    m = jnp.maximum(jnp.max(s, axis=-1, keepdims=True), sink)
    p = jnp.exp(s - m)
    return p / (jnp.sum(p, axis=-1, keepdims=True) + jnp.exp(sink - m))

def _mixer_inputs(x, pos, norm_g, w_in, q_norm_g, k_norm_g):
    b, t, _ = x.shape
    xn = _rmsnorm(x, norm_g)
    q, k, v, b_gate, c_gate, h, g_attn, g_conv = jnp.split(xn @ w_in, SPLITS, axis=-1)
    q = _rope(_rmsnorm(q.reshape(b, t, N_HEADS, HEAD_DIM), q_norm_g), pos)
    k = _rope(_rmsnorm(k.reshape(b, t, N_KV_HEADS, HEAD_DIM), k_norm_g), pos)
    v = v.reshape(b, t, N_KV_HEADS, HEAD_DIM)
    u = c_gate * h
    return q, k, v, u, b_gate, g_attn, g_conv

def _causal_conv(up, conv_w, t):
    return sum(up[:, j:j + t] * conv_w[j] for j in range(CONV_WIDTH))

def _merge_and_ffn(x, attn, conv_y, b_gate, g_attn, g_conv, w_attn_proj, w_conv_proj, w_out,
                   norm_ffn_g, w_ffn_gate, w_ffn_up, w_ffn_down):
    z = b_gate * conv_y
    merged = jax.nn.sigmoid(g_attn) * (attn @ w_attn_proj) + jax.nn.sigmoid(g_conv) * (z @ w_conv_proj)
    x = x + merged @ w_out
    xn = _rmsnorm(x, norm_ffn_g)
    return x + (jax.nn.silu(xn @ w_ffn_gate) * (xn @ w_ffn_up)) @ w_ffn_down

def _banded_window_attention(q, k, v, sinks):
    b, s = q.shape[:2]
    nc = s // CHUNK
    nb = WINDOW_CHUNKS + 1
    pad = ((0, 0), (WINDOW_CHUNKS * CHUNK, 0), (0, 0), (0, 0))
    kp = jnp.pad(k, pad).reshape(b, nc + WINDOW_CHUNKS, CHUNK, N_KV_HEADS, HEAD_DIM)
    vp = jnp.pad(v, pad).reshape(b, nc + WINDOW_CHUNKS, CHUNK, N_KV_HEADS, HEAD_DIM)
    kb = jnp.concatenate([kp[:, j:j + nc] for j in range(nb)], axis=2)
    vb = jnp.concatenate([vp[:, j:j + nc] for j in range(nb)], axis=2)
    qb = q.reshape(b, nc, CHUNK, N_KV_HEADS, GROUP, HEAD_DIM)
    sc = jnp.einsum('bcqkgd,bcskd->bckgqs', qb, kb).astype(jnp.float32) * SCALE
    valid = (jnp.arange(nc)[:, None] + jnp.arange(nb)[None, :]) >= WINDOW_CHUNKS
    valid = jnp.repeat(valid, CHUNK, axis=1)
    sc = jnp.where(valid[None, :, None, None, None, :], sc, NEG_INF)
    sink = sinks.astype(jnp.float32).reshape(N_KV_HEADS, GROUP)[None, None, :, :, None, None]
    probs = _sink_softmax(sc, sink)
    o = jnp.einsum('bckgqs,bcskd->bcqkgd', probs.astype(v.dtype), vb)
    return o.reshape(b, s, D_ATTN)

def _prompt_layer(x, norm_mix_g, w_in, q_norm_g, k_norm_g, attn_sinks, conv_w, w_attn_proj,
                  w_conv_proj, w_out, norm_ffn_g, w_ffn_gate, w_ffn_up, w_ffn_down):
    s = x.shape[1]
    pos = jnp.arange(s)
    q, k, v, u, b_gate, g_attn, g_conv = _mixer_inputs(x, pos, norm_mix_g, w_in, q_norm_g, k_norm_g)
    attn = _banded_window_attention(q, k, v, attn_sinks)
    up = jnp.pad(u, ((0, 0), (CONV_WIDTH - 1, 0), (0, 0)))
    conv_y = _causal_conv(up, conv_w, s)
    y = _merge_and_ffn(x, attn, conv_y, b_gate, g_attn, g_conv, w_attn_proj, w_conv_proj, w_out,
                       norm_ffn_g, w_ffn_gate, w_ffn_up, w_ffn_down)
    return y, k[:, -WINDOW:], v[:, -WINDOW:], up[:, -(CONV_WIDTH - 1):]

def _sample_layer(x, cache_k, cache_v, state_conv, norm_mix_g, w_in, q_norm_g, k_norm_g, attn_sinks,
                  conv_w, w_attn_proj, w_conv_proj, w_out, norm_ffn_g, w_ffn_gate, w_ffn_up, w_ffn_down):
    b, t, _ = x.shape
    pos = PAST_LEN + jnp.arange(t)
    q, k, v, u, b_gate, g_attn, g_conv = _mixer_inputs(x, pos, norm_mix_g, w_in, q_norm_g, k_norm_g)
    kc = jnp.concatenate([cache_k, k], axis=1)
    vc = jnp.concatenate([cache_v, v], axis=1)
    qg = q.reshape(b, t, N_KV_HEADS, GROUP, HEAD_DIM)
    sc = jnp.einsum('bqkgd,bskd->bkgqs', qg, kc).astype(jnp.float32) * SCALE
    sink = attn_sinks.astype(jnp.float32).reshape(N_KV_HEADS, GROUP)[None, :, :, None, None]
    probs = _sink_softmax(sc, sink)
    attn = jnp.einsum('bkgqs,bskd->bqkgd', probs.astype(vc.dtype), vc).reshape(b, t, D_ATTN)
    up = jnp.concatenate([state_conv, u], axis=1)
    conv_y = _causal_conv(up, conv_w, t)
    y = _merge_and_ffn(x, attn, conv_y, b_gate, g_attn, g_conv, w_attn_proj, w_conv_proj, w_out,
                       norm_ffn_g, w_ffn_gate, w_ffn_up, w_ffn_down)
    return y, k, v, up[:, -(CONV_WIDTH - 1):]

def setup_inputs(seed: int = 0) -> dict:
    key = jax.random.key(seed)
    ks = jax.random.split(key, 18)
    win_cache = min(WINDOW, PAST_LEN)

    def nrm(k, shape, scale):
        return jax.random.normal(k, shape, jnp.float32) * scale

    return {
        'x_prompt': nrm(ks[0], (BATCH, SEQ, D_MODEL), 1.0),
        'x_sample': nrm(ks[1], (DEC_BATCH, DEC_SEQ, D_MODEL), 1.0),
        'cache_k': nrm(ks[2], (DEPTH, DEC_BATCH, win_cache, N_KV_HEADS, HEAD_DIM), 1.0),
        'cache_v': nrm(ks[3], (DEPTH, DEC_BATCH, win_cache, N_KV_HEADS, HEAD_DIM), 1.0),
        'state_conv': nrm(ks[4], (DEPTH, DEC_BATCH, CONV_WIDTH - 1, D_CONV), 1.0),
        'norm_mix_g': 1.0 + nrm(ks[5], (DEPTH, D_MODEL), 0.02),
        'w_in': nrm(ks[6], (DEPTH, D_MODEL, D_IN_PROJ), D_MODEL ** -0.5),
        'q_norm_g': 1.0 + nrm(ks[7], (DEPTH, HEAD_DIM), 0.02),
        'k_norm_g': 1.0 + nrm(ks[8], (DEPTH, HEAD_DIM), 0.02),
        'attn_sinks': nrm(ks[9], (DEPTH, N_HEADS), 0.5),
        'conv_w': nrm(ks[10], (DEPTH, CONV_WIDTH, D_CONV), CONV_WIDTH ** -0.5),
        'w_attn_proj': nrm(ks[11], (DEPTH, D_ATTN, D_MODEL), D_ATTN ** -0.5),
        'w_conv_proj': nrm(ks[12], (DEPTH, D_CONV, D_MODEL), D_CONV ** -0.5),
        'w_out': nrm(ks[13], (DEPTH, D_MODEL, D_MODEL), D_MODEL ** -0.5),
        'norm_ffn_g': 1.0 + nrm(ks[14], (DEPTH, D_MODEL), 0.02),
        'w_ffn_gate': nrm(ks[15], (DEPTH, D_MODEL, D_FF), D_MODEL ** -0.5),
        'w_ffn_up': nrm(ks[16], (DEPTH, D_MODEL, D_FF), D_MODEL ** -0.5),
        'w_ffn_down': nrm(ks[17], (DEPTH, D_FF, D_MODEL), D_FF ** -0.5),
    }

def reference(x_prompt, x_sample, cache_k, cache_v, state_conv, norm_mix_g, w_in, q_norm_g, k_norm_g,
              attn_sinks, conv_w, w_attn_proj, w_conv_proj, w_out, norm_ffn_g, w_ffn_gate, w_ffn_up,
              w_ffn_down):
    yp, ys = x_prompt, x_sample
    kp_l, vp_l, cp_l, ks_l, vs_l, cs_l = [], [], [], [], [], []
    for l in range(DEPTH):
        w = (norm_mix_g[l], w_in[l], q_norm_g[l], k_norm_g[l], attn_sinks[l], conv_w[l],
             w_attn_proj[l], w_conv_proj[l], w_out[l], norm_ffn_g[l], w_ffn_gate[l], w_ffn_up[l],
             w_ffn_down[l])
        yp, kp, vp, cp = _prompt_layer(yp, *w)
        ys, ksn, vsn, csn = _sample_layer(ys, cache_k[l], cache_v[l], state_conv[l], *w)
        kp_l.append(kp); vp_l.append(vp); cp_l.append(cp)
        ks_l.append(ksn); vs_l.append(vsn); cs_l.append(csn)
    return (yp, ys, jnp.stack(kp_l), jnp.stack(vp_l), jnp.stack(cp_l),
            jnp.stack(ks_l), jnp.stack(vs_l), jnp.stack(cs_l))


_drawn_inputs = setup_inputs


def setup_inputs(seed=0):
    import zlib

    import numpy as np

    out = dict(_drawn_inputs(seed))
    spreads = {}
    factors = {'q_norm_g': 8.0,
     'k_norm_g': 2.97,
     'attn_sinks': 64.0,
     'norm_ffn_g': 4.174,
     'cache_v': 9.972}
    for name, (base, spread) in spreads.items():
        noise = np.random.default_rng([zlib.crc32(name.encode()), seed]).standard_normal(out[name].shape)
        drawn = base * np.exp(spread * noise) if base else spread * noise
        out[name] = __import__('jax').numpy.asarray(drawn.astype(out[name].dtype))
    for name, factor in factors.items():
        out[name] = (out[name] * factor).astype(out[name].dtype)
    return out
```

```python
from contextlib import ExitStack

import numpy as np

import concourse.bass as bass
from concourse import mybir
from concourse.alu_op_type import AluOpType as ALU

F32 = mybir.dt.float32
F32R = mybir.dt.float32r
ACT = mybir.ActivationFunctionType
AX_X = mybir.AxisListType.X

P = 128
CHUNK = 64
HEAD_DIM = 64
ROPE_THETA = 10000.0
EPS = 1e-6
NEG_INF = -1e30
SCALE = HEAD_DIM ** -0.5
GROUP_COLS = 256
SLOTS = 4


class OwnSteps:

    def __init__(self, engine, semaphore):
        self.engine, self.semaphore, self.base, self.count = engine, semaphore, 0, 0

    def mark(self, instruction):
        instruction.then_inc(self.semaphore, 1)
        self.count += 1

    def settle(self):
        self.engine.wait_ge(self.semaphore, self.base + self.count)

    def begin_loop(self, j, per):
        self.outer = self.base + self.count
        self.base, self.count, self.per = self.outer + per * j, 0, per

    def end_loop(self, times):
        assert self.count == self.per, (self.count, self.per)
        self.base, self.count = self.outer + self.per * times, 0


def encoder_layer(nc, x_prompt, x_sample, cache_k, cache_v, state_conv, norm_mix_g, w_in, q_norm_g,
                  k_norm_g, attn_sinks, conv_w, w_attn_proj, w_conv_proj, w_out, norm_ffn_g,
                  w_ffn_gate, w_ffn_up, w_ffn_down, constants, y_prompt, y_sample, new_k_prompt,
                  new_v_prompt, new_conv_prompt, new_k_sample, new_v_sample, new_conv_sample):
    D = x_prompt.shape[2]
    TP, TS = x_prompt.shape[1], x_sample.shape[1]
    T = TP + TS
    KV_HEADS = cache_k.shape[3]
    D_KV = KV_HEADS * HEAD_DIM
    D_FF = w_ffn_gate.shape[2]
    BLOCKS = D // P
    PAIRS = D // GROUP_COLS
    PAST = cache_k.shape[2]
    assert PAST == P and TP == 2 * P and D_KV == GROUP_COLS and T <= 512 and KV_HEADS == 4
    assert BLOCKS == 4 * SLOTS

    COL_Q, COL_K = 0, D // GROUP_COLS
    COL_V = COL_K + 1
    COL_B = COL_V + 1
    COL_C, COL_H, COL_GA, COL_GC = (COL_B + PAIRS * n for n in (1, 2, 3, 4))

    FFN_PARTS = []
    left = D_FF // GROUP_COLS
    while left:
        n = min(PAIRS, left)
        FFN_PARTS.append((n, n * 2 // SLOTS))
        left -= n

    G_K, G_V, G_MIX = 0, 1, 2
    G_ATT = G_MIX + 4 * PAIRS
    G_CONV = G_ATT + 2 * PAIRS
    G_OUT = G_CONV + 2 * PAIRS
    G_FFN = [G_OUT + PAIRS]
    for n, _ in FFN_PARTS:
        G_FFN.append(G_FFN[-1] + 2 * n + PAIRS)
    G_END = G_FFN[-1]

    PARAMS = 7 * BLOCKS + 2

    with ExitStack() as ctx:
        def sb(name, shape, dt=F32):
            return ctx.enter_context(nc.sbuf_tensor(name, shape, dt))

        def sem(name):
            return ctx.enter_context(nc.semaphore(name))

        raw = sb("raw", [P, SLOTS, 4, GROUP_COLS])
        w_hi = sb("w_hi", [P, SLOTS, 4, GROUP_COLS], F32R)
        w_lo = sb("w_lo", [P, SLOTS, 4, GROUP_COLS], F32R)
        xn_hi, xn_lo = sb("xn_hi", [P, BLOCKS, T], F32R), sb("xn_lo", [P, BLOCKS, T], F32R)
        at_hi, at_lo = sb("at_hi", [P, BLOCKS, T], F32R), sb("at_lo", [P, BLOCKS, T], F32R)
        z_hi, z_lo = sb("z_hi", [P, BLOCKS, T], F32R), sb("z_lo", [P, BLOCKS, T], F32R)
        region_x = sb("region_x", [P, BLOCKS * T])
        region_m = sb("region_m", [P, BLOCKS * T])

        def pairs_of(t):
            return t[:].rearrange("p (j t) n -> p j t n", t=2)

        xn_hi_p, xn_lo_p, at_hi_p, at_lo_p, z_hi_p, z_lo_p = map(pairs_of, (xn_hi, xn_lo, at_hi, at_lo, z_hi, z_lo))
        residual_p = region_x[:].rearrange("p (j t n) -> p j t n", t=2, n=T)
        gated_attn_p = region_m[:].rearrange("p (j t n) -> p j t n", t=2, n=T)

        def carve(region, at, *dims):
            n = int(np.prod(dims))
            ap = region[:, at:at + n]
            if len(dims) == 2:
                ap = ap.rearrange("p (a b) -> p a b", b=dims[1])
            elif len(dims) == 3:
                ap = ap.rearrange("p (a b c) -> p a b c", b=dims[1], c=dims[2])
            return ap, at + n

        KEYS = TP + PAST + TS
        keys_all, o = carve(region_x, 0, KV_HEADS, KEYS)
        values_all, o = carve(region_x, o, KV_HEADS, 4, HEAD_DIM)
        probs, o_p = carve(region_x, o, 4, 3 * P)
        probs_sample, o = carve(region_x, o_p, PAST + TS)
        k_rows, _ = carve(region_x, o_p - 4 * 3 * P, 2, D_KV)
        head_a, o = carve(region_m, 0, 2, T)
        head_b, o = carve(region_m, o, 2, T)
        head_c, o = carve(region_m, o, 2, T)
        c_gate, o = carve(region_m, o, 2, T)
        UP = 2 + TP + 2 + TS
        conv_in, o = carve(region_m, o, 2, UP)
        conv_y, o = carve(region_m, o, 2, UP - 2)
        probs_t, o_s = carve(region_m, o, 2, 3 * P)
        probs_t_sample, _ = carve(region_m, o_s, 2, P)
        params, _ = carve(region_m, o, P)
        cache_k_rows, _ = carve(region_m, o + P, D_KV)
        more_squares, o = carve(region_m, D + D // SLOTS, D // SLOTS)
        diagonals = [carve(region_m, o + n * P, P)[0] for n in range(3)]
        x_rows = [region_x[:, 0:D], region_x[:, D:2 * D], region_m[0:TS, 0:D]]
        x_rows_prompt = region_x[:, 0:2 * D].rearrange("p (a n) -> p a n", a=2)
        row_squares, _ = carve(region_m, D, D // SLOTS)
        gate, o = carve(region_x, 0, 2, T)
        product, _ = carve(region_x, o, 2, T)
        squares, o = carve(region_m, 0, 2, T)
        square_sum, o = carve(region_m, o, 2, T)
        silu, o = carve(region_m, o, 2, T)
        hidden, o = carve(region_m, o, 2, T)
        inv_rms, o = carve(region_m, o, T)
        y_rows, o = carve(region_m, o, 3, GROUP_COLS)
        y_cols = silu
        x_res = y_rows

        keys_cur = sb("keys_cur", [P, KEYS])
        values_cur = sb("values_cur", [P, 4, HEAD_DIM])
        out_heads = sb("out_heads", [P, 2, 4, HEAD_DIM])
        q_sample = sb("q_sample", [P, 2, 2, TS])
        out_sample = sb("out_sample", [P, HEAD_DIM])
        out_sample_t = sb("out_sample_t", [P, 2, TS])
        consts = sb("consts", [P, constants.shape[1]])
        ident, ones, eps = consts[:, 0:P], consts[:, P:2 * P], consts[:, 2 * P:2 * P + 1]
        o = 2 * P + 1
        cos, sin = consts[:, o:o + T], consts[:, o + T:o + 2 * T]
        o += 2 * T
        same_head = consts[:, o:o + P]
        mask = consts[:, o + P:o + 4 * P]
        FIRST_CONSTS = 2 * P + 1
        param_cols = sb("param_cols", [P, PARAMS])
        conv_tail = sb("conv_tail", [P, 4, BLOCKS])
        conv_tail_rows = sb("conv_tail_rows", [4 * BLOCKS, P])
        sinks_all = sb("sinks_all", [P, 4 * PAIRS])
        sinks_sample_all = sb("sinks_sample_all", [P, PAIRS])
        sinks_cur = sb("sinks_cur", [P, 5])
        conv_w_cur = sb("conv_w_cur", [P, 3, 2])
        state_cur = sb("state_cur", [P, 2, 2])
        stats = sb("stats", [P, 48])
        s_max, s_neg, s_sink, s_sum, s_inv = (stats[:, 8 * n:8 * n + 8] for n in range(5))
        m_max, m_neg, m_sink, m_sum, m_inv = (stats[:, 40 + n:41 + n] for n in range(5))
        square_parts = sb("square_parts", [P, 3, SLOTS])
        norm_stats = sb("norm_stats", [P, 3])
        in_rms = sb("in_rms", [P, T])

        def wait_apart(engine, semaphore, value):
            engine.wait_ge(semaphore, value)
            engine.sem_inc(S["waits_passed"])

        acc = ctx.enter_context(nc.psum_tensor("acc", [P, 4, 512], F32))
        side = ctx.enter_context(nc.psum_tensor("side", [P, 4, 512], F32))

        raw_loaded = [sem(f"raw_loaded{s}") for s in range(SLOTS)]
        names = """hi_ready lo_ready piece_done first_consts_loaded consts_loaded params_loaded cache_k_loaded
            cache_v_loaded x_squared x_rms_ready diagonal_ready in_rms_in_psum in_rms_ready first_params_loaded gain_in_psum gain_ready x_transposed xn_hi_ready xn_ready param_cols_in_psum
            param_cols_ready cache_k_in_psum vector_steps scalar_steps q_scaled q_squared ssq_ready rms_ready
            q_roped q_sample_packed k_rows_in_psum k_rows_ready v_in_psum values_ready
            kv_stored keys_filled v_region_free kv_staged c_copied scores_ready scores_masked neg_max_ready probs_ready
            probs_in_psum probs_copied out_in_psum out_normed out_t_in_psum out_sample_copied
            attn_hi_ready side_free z_product_ready z_hi_ready z_ready gate_scaled gate_ready product_ready
            merged_hi_ready merged_ready x_res_loaded x_res_in_psum x_res_copied residual_ready
            squared square_sum_ready mean_in_psum ffn_rms_ready ffn_hi_ready ffn_in_ready gate_product_ready
            silu_ready hidden_product_ready hidden_hi_ready hidden_ready y_ready y_in_psum y_rows_ready
            y_stored tails_in_psum tails_ready tails_stored sinks_staged pool_steps waits_passed""".split()
        S = {n: sem(n) for n in names}
        x_loaded = [sem(f"x_loaded{n}") for n in range(SLOTS)]
        acc_free = [sem("acc_free_even"), sem("acc_free_odd")]

        w_in_b = w_in[0].rearrange("(s k p) (c n) -> s p k c n", k=4, p=P, n=GROUP_COLS)
        square_w = [w[0].rearrange("(s k p) (c n) -> s p k c n", k=4, p=P, n=GROUP_COLS)
                    for w in (w_attn_proj, w_conv_proj, w_out, w_ffn_gate, w_ffn_up)]
        attn_proj_b, conv_proj_b, out_b, ffn_gate_b, ffn_up_b = square_w

        block = ctx.enter_context(nc.Block())

        @block.sync
        def _(sp):
            def load(g, source, blocks=4, slots=range(SLOTS)):
                for s in slots:
                    if not (isinstance(g, int) and g == 0):
                        sp.wait_ge(S["lo_ready"], 4 * g + (s - 3))
                    sp.dma_start(raw[:, s, 0:blocks], source(s)).then_inc(raw_loaded[s], 16)

            xp = x_prompt[0].rearrange("(a p) n -> p a n", p=P)
            for s in range(SLOTS):
                quarter = slice(s * D // SLOTS, (s + 1) * D // SLOTS)
                sp.dma_start(x_rows_prompt[:, :, quarter], xp[:, :, quarter]).then_inc(x_loaded[s], 16)
                sp.dma_start(x_rows[2][:, quarter], x_sample[0][:, quarter]).then_inc(x_loaded[s], 16)
                load(G_K, lambda s: w_in_b[s, :, :, COL_K, :], slots=[s])
            load(G_V, lambda s: w_in_b[s, :, :, COL_V, :])
            with sp.Fori(0, PAIRS) as j:
                for n, col in enumerate((COL_Q, COL_C, COL_H, COL_B)):
                    load(G_MIX + n + 4 * j, lambda s: w_in_b[s, :, :, col + j, :])
            for first, col, proj in ((G_ATT, COL_GA, attn_proj_b), (G_CONV, COL_GC, conv_proj_b)):
                with sp.Fori(0, PAIRS) as j:
                    load(first + 2 * j, lambda s: w_in_b[s, :, :, col + j, :])
                    load(first + 1 + 2 * j, lambda s: proj[s, :, :, j, :])
            with sp.Fori(0, PAIRS) as j:
                load(G_OUT + j, lambda s: out_b[s, :, :, j, :])
            for part, (cols, blocks) in enumerate(FFN_PARTS):
                with sp.Fori(0, cols) as i:
                    load(G_FFN[part] + 2 * i, lambda s: ffn_gate_b[s, :, :, PAIRS * part + i, :])
                    load(G_FFN[part] + 1 + 2 * i, lambda s: ffn_up_b[s, :, :, PAIRS * part + i, :])
                down = w_ffn_down[0, D * part:D * part + SLOTS * blocks * P, :].rearrange(
                    "(s k p) (c n) -> s p k c n", k=blocks, p=P, n=GROUP_COLS)
                with sp.Fori(0, PAIRS) as j:
                    load(G_FFN[part] + 2 * cols + j, lambda s: down[s, :, :, j, :], blocks)

        @block.gpsimd
        def _(pool):
            own = OwnSteps(pool, S["pool_steps"])

            def in_turn(instruction):
                own.mark(instruction)
                own.settle()

            in_turn(nc.gpsimd.memset(q_sample[:], 0.0))
            row = BLOCKS
            for source in (norm_ffn_g[0], conv_w[0], state_conv[0, 0]):
                flat = source.rearrange("(a b) -> a b", b=P) if len(source.shape) == 1 else \
                    source.rearrange("r (a b) -> (r a) b", b=P)
                n = flat.shape[0]
                pool.dma_start(params[row:row + n, :], flat).then_inc(S["params_loaded"], 16)
                row += n
            for source in (q_norm_g, k_norm_g):
                for half in range(2):
                    pool.dma_start(params[row:row + 1, half * HEAD_DIM:(half + 1) * HEAD_DIM],
                                   source).then_inc(S["params_loaded"], 16)
                row += 1
            pool.dma_start(cache_k_rows, cache_k[0, 0].rearrange("s k d -> s (k d)")).then_inc(S["cache_k_loaded"], 16)
            pool.dma_start(sinks_all[:], attn_sinks[0].partition_broadcast(P)).then_inc(S["sinks_staged"], 16)
            pool.wait_ge(S["sinks_staged"], 16)
            sinks_by_head = sinks_all[:].rearrange("p (j h) -> p h j", h=4)
            for half in range(2):
                for tile in range(2):
                    r = 64 * half + 32 * tile
                    in_turn(nc.gpsimd.tensor_copy(sinks_sample_all[r:r + 32, :],
                                                  sinks_by_head[r:r + 32, 2 * tile + half, :]))
            pool.wait_ge(S["v_region_free"], 1)
            pool.dma_start(values_all[:, :, 2, :], cache_v[0, 0]).then_inc(S["cache_v_loaded"], 16)
            pool.wait_ge(S["k_rows_ready"], 1)
            pool.dma_start(new_k_prompt[0, 0].rearrange("s k d -> s (k d)"), k_rows[:, 0, :]).then_inc(S["kv_stored"], 16)
            pool.dma_start(new_k_sample[0, 0].rearrange("s k d -> s (k d)"), k_rows[0:TS, 1, :]).then_inc(S["kv_stored"], 16)
            pool.wait_ge(S["values_ready"], 1)
            pool.dma_start(new_v_prompt[0, 0], values_all[:, :, 1, :]).then_inc(S["kv_stored"], 16)
            pool.dma_start(new_v_sample[0, 0], values_all[0:TS, :, 3, :]).then_inc(S["kv_stored"], 16)
            pool.wait_ge(S["kv_stored"], 64)
            pool.wait_ge(S["keys_filled"], 1)
            pool.wait_ge(S["cache_v_loaded"], 16)
            conv_w_all = param_cols[:, 2 * BLOCKS:5 * BLOCKS].rearrange("p (w j t) -> p w j t", w=3, t=2)
            state_all = param_cols[:, 5 * BLOCKS:7 * BLOCKS].rearrange("p (r j t) -> p r j t", r=2, t=2)

            def stage(head, j):
                wait_apart(pool, S["side_free"], j + 1)
                for to, of in (
                        (keys_cur[:], keys_all[:, head, :]),
                        (values_cur[:], values_all[:, head, :, :]),
                        (sinks_cur[:, 0:4], sinks_all[:].rearrange("p (j h) -> p j h", h=4)[:, j, :]),
                        (sinks_cur[:, 4:5], sinks_sample_all[:].rearrange("p (j o) -> p j o", o=1)[:, j, :]),
                        (conv_w_cur[:], conv_w_all[:, :, j, :]),
                        (state_cur[:], state_all[:, :, j, :])):
                    own.mark(nc.gpsimd.tensor_copy(to, of))
                    own.settle()
                    pool.sem_inc(S["waits_passed"])
                nc.gpsimd.sem_inc(S["kv_staged"])

            with pool.Fori(0, KV_HEADS) as head:
                own.begin_loop(head, 12)
                stage(head, 2 * head)
                stage(head, 2 * head + 1)
                own.end_loop(KV_HEADS)

            xp = x_prompt[0].rearrange("(a p) (j n) -> p a j n", p=P, n=GROUP_COLS)
            xs = x_sample[0].rearrange("p (j n) -> p j n", n=GROUP_COLS)

            def load_residual(j):
                pool.dma_start(x_res[:, 0:2, :], xp[:, :, j, :]).then_inc(S["x_res_loaded"], 16)
                pool.dma_start(x_res[0:TS, 2, :], xs[:, j, :]).then_inc(S["x_res_loaded"], 16)

            pool.wait_ge(S["merged_ready"], PAIRS)
            load_residual(0)
            pool.wait_ge(S["tails_ready"], 1)
            for n, out in enumerate((new_conv_prompt, new_conv_sample)):
                pool.dma_start(out[0, 0].rearrange("r (b p) -> (r b) p", p=P),
                               conv_tail_rows[2 * BLOCKS * n:2 * BLOCKS * (n + 1), :]).then_inc(S["tails_stored"], 16)
            with pool.Fori(1, PAIRS) as j:
                pool.wait_ge(S["x_res_in_psum"], j)
                load_residual(j)
            pool.wait_ge(S["tails_stored"], 32)

        @block.scalar
        def _(act):
            own = OwnSteps(act, S["scalar_steps"])
            act.dma_start(consts[:, 0:FIRST_CONSTS], constants[:, 0:FIRST_CONSTS]).then_inc(S["first_consts_loaded"], 16)
            act.dma_start(params[0:BLOCKS, :], norm_mix_g[0].rearrange("(a b) -> a b", b=P)
                          ).then_inc(S["first_params_loaded"], 16)
            act.dma_start(consts[:, FIRST_CONSTS:], constants[:, FIRST_CONSTS:]).then_inc(S["consts_loaded"], 16)

            def ahead(g, s):
                act.wait_ge(raw_loaded[s], 16 * g + 16)
                if not (isinstance(g, int) and g == 0):
                    act.wait_ge(S["piece_done"], 4 * g + (s - 3))
                nc.scalar.activation(w_hi[:, s], raw[:, s], ACT.Copy).then_inc(S["hi_ready"], 1)

            def group_done(g):
                act.wait_ge(S["piece_done"], 4 * g + 4)

            act.wait_ge(S["gain_ready"], 1)
            for s in range(SLOTS):
                for k in range(4 * s, 4 * s + 4):
                    act.wait_ge(S["x_transposed"], k + 1)
                    nc.scalar.activation(xn_hi[:, k], side[:, k % 4, 0:T], ACT.Copy,
                                         scale=param_cols[:, k:k + 1]).then_inc(S["xn_hi_ready"], 1)
                ahead(G_K, s)
                for n in (0, 2):
                    r = x_rows[n].shape[0]
                    if s or n:
                        own.settle()
                    own.mark(nc.scalar.activation(row_squares[0:r], x_rows[n][:, s * D // SLOTS:(s + 1) * D // SLOTS],
                                                  ACT.Square, accum_out=square_parts[0:r, n, s:s + 1]))
            own.settle()
            act.sem_inc(S["x_squared"])
            ahead(G_V, 0)
            act.wait_ge(S["x_squared"], 2)
            nc.scalar.activation(norm_stats[:, 0:2], norm_stats[:, 0:2], ACT.Sqrt, bias=eps, scale=1.0 / D)
            nc.scalar.activation(norm_stats[0:TS, 2:3], norm_stats[0:TS, 2:3], ACT.Sqrt, bias=eps[0:TS],
                                 scale=1.0 / D).then_inc(S["x_rms_ready"], 1)

            def square(count):
                act.wait_ge(S["q_scaled"], count)
                nc.scalar.activation(head_b, head_a, ACT.Square).then_inc(S["q_squared"], 1)

            def head_rms(count):
                act.wait_ge(S["ssq_ready"], count)
                nc.scalar.activation(head_c, side[:, 0:2, 0:T], ACT.Sqrt, bias=eps,
                                     scale=1.0 / HEAD_DIM).then_inc(S["rms_ready"], 1)

            for s in range(1, SLOTS):
                ahead(G_V, s)
            square(1)
            ahead(G_MIX, 0)
            head_rms(1)
            ahead(G_MIX, 1)
            ahead(G_MIX, 2)
            act.wait_ge(S["k_rows_in_psum"], 1)
            nc.scalar.activation(k_rows[:, 0, :], side[:, 2, 0:D_KV], ACT.Copy)
            nc.scalar.activation(k_rows[0:TS, 1, :], side[0:TS, 3, 0:D_KV], ACT.Copy).then_inc(S["k_rows_ready"], 1)

            with act.Fori(0, PAIRS) as j:
                g = G_MIX + 4 * j
                ahead(g, 3)
                ahead(g + 1, 0)
                ahead(g + 1, 1)
                ahead(g + 1, 2)
                square(j + 2)
                ahead(g + 1, 3)
                head_rms(j + 2)
                ahead(g + 2, 0)
                ahead(g + 2, 1)
                ahead(g + 2, 2)
                ahead(g + 2, 3)
                ahead(g + 3, 0)
                act.wait_ge(S["neg_max_ready"], 2 * j + 1)
                for u in range(4):
                    for half, lo, hi in ((0, 0, P), (1, P, 3 * P)):
                        c = 4 * half + u
                        nc.scalar.activation(probs[:, u, lo:hi], probs[:, u, lo:hi], ACT.Exp,
                                             bias=s_neg[:, c:c + 1], accum_out=s_sum[:, c:c + 1])
                nc.scalar.activation(s_sink, s_sink, ACT.Exp).then_inc(S["probs_ready"], 1)
                ahead(g + 3, 1)
                act.wait_ge(S["neg_max_ready"], 2 * j + 2)
                nc.scalar.activation(probs_sample, side[:, 0, 0:PAST + TS], ACT.Exp, bias=m_neg, scale=SCALE,
                                     accum_out=m_sum)
                nc.scalar.activation(m_sink, m_sink, ACT.Exp).then_inc(S["probs_ready"], 1)
                ahead(g + 3, 2)
                for u in range(2):
                    act.wait_ge(S["probs_in_psum"], 5 * j + u + 1)
                    nc.scalar.activation(probs_t[:, u], side[:, 1 + u, 0:3 * P], ACT.Copy).then_inc(S["probs_copied"], 1)
                ahead(g + 3, 3)
                for u in range(2):
                    act.wait_ge(S["probs_in_psum"], 5 * j + u + 3)
                    nc.scalar.activation(probs_t[:, u], side[:, 3 * (1 - u), 0:3 * P], ACT.Copy).then_inc(S["probs_copied"], 1)
                ahead(g + 4, 0)
                act.wait_ge(S["probs_in_psum"], 5 * j + 5)
                nc.scalar.activation(probs_t_sample[:, 0], side[:, 2, 0:P], ACT.Copy)
                nc.scalar.activation(probs_t_sample[0:TS, 1], side[0:TS, 2, P:2 * P], ACT.Copy).then_inc(S["probs_copied"], 1)
                ahead(g + 4, 1)
                ahead(g + 4, 2)
                wait_apart(act, S["z_product_ready"], j + 1)
                nc.scalar.activation(z_hi_p[:, j], c_gate, ACT.Copy).then_inc(S["z_hi_ready"], 1)
                wait_apart(act, S["out_t_in_psum"], j + 1)
                nc.scalar.activation(at_hi_p[:, j, :, 0:TP], side[:, 0, :].rearrange("p (t n) -> p t n", t=2), ACT.Copy)
                wait_apart(act, S["out_sample_copied"], j + 1)
                nc.scalar.activation(at_hi_p[:, j, :, TP:T], out_sample_t[:], ACT.Copy).then_inc(S["attn_hi_ready"], 1)

            def sigmoid_gate(count):
                act.wait_ge(S["gate_scaled"], count)
                nc.scalar.activation(gate, gate, ACT.Sigmoid).then_inc(S["gate_ready"], 1)

            with act.Fori(0, PAIRS) as j:
                g = G_ATT + 2 * j
                ahead(g, 3)
                ahead(g + 1, 0)
                ahead(g + 1, 1)
                ahead(g + 1, 2)
                sigmoid_gate(j + 1)
                ahead(g + 1, 3)
                ahead(g + 2, 0)
                ahead(g + 2, 1)
                ahead(g + 2, 2)
            with act.Fori(0, PAIRS) as j:
                g = G_CONV + 2 * j
                ahead(g, 3)
                ahead(g + 1, 0)
                ahead(g + 1, 1)
                ahead(g + 1, 2)
                sigmoid_gate(j + PAIRS + 1)
                ahead(g + 1, 3)
                ahead(g + 2, 0)
                ahead(g + 2, 1)
                ahead(g + 2, 2)
                wait_apart(act, S["product_ready"], j + 1)
                nc.scalar.activation(at_hi_p[:, j], product, ACT.Copy).then_inc(S["merged_hi_ready"], 1)

            act.wait_ge(S["tails_in_psum"], 1)
            nc.scalar.activation(conv_tail_rows[:], side[0:4 * BLOCKS, 2, 0:P], ACT.Copy).then_inc(S["tails_ready"], 1)
            ffn_gain = param_cols[:, BLOCKS:2 * BLOCKS].rearrange("p (j t o) -> p j t o", t=2, o=1)
            with act.Fori(0, PAIRS) as j:
                g = G_OUT + j
                ahead(g, 3)
                ahead(g + 1, 0)
                ahead(g + 1, 1)
                wait_apart(act, S["x_res_in_psum"], j + 1)
                nc.scalar.activation(residual_p[:, j, :, 0:2 * P], side[:, 0, :].rearrange("p (t n) -> p t n", t=2),
                                     ACT.Copy)
                nc.scalar.activation(residual_p[:, j, :, TP:T], side[:, 1, 0:2 * TS].rearrange("p (t n) -> p t n", t=2),
                                     ACT.Copy).then_inc(S["x_res_copied"], 1)
                ahead(g + 1, 2)
                wait_apart(act, S["residual_ready"], j + 1)
                for t in range(2):
                    last = nc.scalar.activation(xn_hi_p[:, j, t], residual_p[:, j, t], ACT.Copy,
                                                scale=ffn_gain[:, j, t])
                last.then_inc(S["ffn_hi_ready"], 1)
                nc.scalar.activation(squares, residual_p[:, j], ACT.Square).then_inc(S["squared"], 1)

            done_pairs = 0
            for part, (cols, _) in enumerate(FFN_PARTS):
                if part == 0:
                    act.wait_ge(S["mean_in_psum"], 1)
                    nc.scalar.activation(inv_rms, side[:, 3, 0:T], ACT.Sqrt, bias=eps, scale=1.0 / D
                                         ).then_inc(S["ffn_rms_ready"], 1)
                with act.Fori(0, cols) as i:
                    g = G_FFN[part] + 2 * i
                    ahead(g, 3)
                    ahead(g + 1, 0)
                    ahead(g + 1, 1)
                    ahead(g + 1, 2)
                    act.wait_ge(S["gate_product_ready"], done_pairs + i + 1)
                    nc.scalar.activation(silu, silu, ACT.Silu).then_inc(S["silu_ready"], 1)
                    ahead(g + 1, 3)
                    ahead(g + 2, 0)
                    ahead(g + 2, 1)
                    ahead(g + 2, 2)
                    wait_apart(act, S["hidden_product_ready"], done_pairs + i + 1)
                    nc.scalar.activation(at_hi_p[:, i], hidden, ACT.Copy).then_inc(S["hidden_hi_ready"], 1)
                done_pairs += cols
                g_down = G_FFN[part] + 2 * cols
                if part < len(FFN_PARTS) - 1:
                    with act.Fori(0, PAIRS) as j:
                        g = g_down + j
                        ahead(g, 3)
                        ahead(g + 1, 0)
                        ahead(g + 1, 1)
                        ahead(g + 1, 2)

            yp = y_prompt[0].rearrange("(a p) (j n) -> p a j n", p=P, n=GROUP_COLS)
            ys = y_sample[0].rearrange("p (j n) -> p j n", n=GROUP_COLS)

            def store_y(j, first=False):
                act.wait_ge(S["y_in_psum"], j + 1)
                if not first:
                    act.wait_ge(S["y_stored"], 32 * j)
                nc.scalar.activation(y_rows[:, 0:2, :], side[:, 0, :].rearrange("p (a n) -> p a n", a=2), ACT.Copy)
                nc.scalar.activation(y_rows[0:TS, 2, :], side[0:TS, 1, 0:GROUP_COLS], ACT.Copy).then_inc(S["y_rows_ready"], 1)
                act.wait_ge(S["y_rows_ready"], j + 1)
                act.dma_start(yp[:, :, j, :], y_rows[:, 0:2, :]).then_inc(S["y_stored"], 16)
                act.dma_start(ys[:, j, :], y_rows[0:TS, 2, :]).then_inc(S["y_stored"], 16)

            for s in range(3):
                ahead(g_down + (s + 3) // 4, (s + 3) % 4)
            ahead(g_down + 1, 2)
            ahead(g_down + 1, 3)
            ahead(g_down + 2, 0)
            store_y(0, first=True)
            ahead(g_down + 2, 1)
            ahead(g_down + 2, 2)
            with act.Fori(1, PAIRS - 2) as j:
                g = g_down + 1 + j
                ahead(g, 3)
                ahead(g + 1, 0)
                store_y(j)
                ahead(g + 1, 1)
                ahead(g + 1, 2)
            ahead(g_down + PAIRS - 1, 3)
            store_y(PAIRS - 2)
            store_y(PAIRS - 1)
            act.wait_ge(S["y_stored"], 32 * PAIRS)

        @block.vector
        def _(dve):
            own = OwnSteps(dve, S["vector_steps"])
            V = nc.vector

            def ahead(g, s):
                dve.wait_ge(S["hi_ready"], 4 * g + s + 1)
                V.tensor_tensor(w_lo[:, s], raw[:, s], w_hi[:, s].bitcast(F32), ALU.subtract).then_inc(S["lo_ready"], 1)

            def group_done(g):
                dve.wait_ge(S["piece_done"], 4 * g + 4)

            def wide(ap, *shape):
                return ap.broadcast_to(list(shape))

            dve.wait_ge(S["gain_in_psum"], 1)
            V.tensor_copy(param_cols[:, 0:BLOCKS], acc[:, 3, 0:BLOCKS]).then_inc(S["gain_ready"], 1)
            dve.wait_ge(S["gain_ready"], 1)
            for s in range(SLOTS):
                for k in range(4 * s, 4 * s + 4):
                    dve.wait_ge(S["xn_hi_ready"], k + 1)
                    V.scalar_tensor_tensor(out=xn_lo[:, k], in0=side[:, k % 4, 0:T], scalar=param_cols[:, k:k + 1],
                                           in1=xn_hi[:, k].bitcast(F32), op0=ALU.mult,
                                           op1=ALU.subtract).then_inc(S["xn_ready"], 1)
                ahead(G_K, s)
                rows = x_rows[1][:, s * D // SLOTS:(s + 1) * D // SLOTS]
                if s:
                    own.settle()
                own.mark(V.tensor_tensor_reduce(out=more_squares, in0=rows, in1=rows, scale=1.0, scalar=0.0,
                                                op0=ALU.mult, op1=ALU.add, accum_out=square_parts[:, 1, s:s + 1]))
            own.settle()
            dve.wait_ge(S["x_squared"], 1)
            V.reduce_sum(norm_stats[:, 0:2], square_parts[:, 0:2], AX_X)
            own.mark(V.reduce_sum(norm_stats[0:TS, 2:3], square_parts[0:TS, 2:3], AX_X))
            own.settle()
            dve.sem_inc(S["x_squared"])
            ahead(G_V, 0)
            V.memset(values_all[:, :, 3, :], 0.0).then_inc(S["v_region_free"], 1)
            own.mark(V.memset(conv_in[:, :, 0:2], 0.0))
            dve.wait_ge(S["x_rms_ready"], 1)
            V.reciprocal(norm_stats[:, 0:2], norm_stats[:, 0:2])
            own.mark(V.reciprocal(norm_stats[0:TS, 2:3], norm_stats[0:TS, 2:3]))
            own.settle()
            for n, r in enumerate((P, P, TS)):
                last = V.tensor_scalar(diagonals[n][0:r, 0:r], ident[0:r, 0:r], norm_stats[0:r, n:n + 1], None, ALU.mult)
            last.then_inc(S["diagonal_ready"], 1)

            def over_rms(out, psum):
                return V.tensor_tensor(out, psum, wide(in_rms[:].unsqueeze(1), P, 2, T), ALU.mult)

            def rope(count, gain):
                dve.wait_ge(S["rms_ready"], count)
                own.mark(V.reciprocal(head_c, head_c))
                own.settle()
                own.mark(V.scalar_tensor_tensor(out=head_b, in0=head_a, scalar=gain, in1=head_c, op0=ALU.mult,
                                                op1=ALU.mult))
                own.settle()
                for q in range(4):
                    src, dst = 32 * q, 32 * (q ^ 1)
                    V.tensor_tensor(head_c[dst:dst + 32], head_b[src:src + 32],
                                    wide(sin[src:src + 32].unsqueeze(1), 32, 2, T), ALU.mult)
                own.mark(V.tensor_tensor(head_a, head_b, wide(cos.unsqueeze(1), P, 2, T), ALU.mult))
                own.settle()
                V.tensor_tensor(head_a, head_a, head_c, ALU.add).then_inc(S["q_roped"], 1)
                dve.wait_ge(S["q_roped"], count)

            q_gain, k_gain = (param_cols[:, 7 * BLOCKS + n:7 * BLOCKS + n + 1] for n in range(2))

            def scaled_heads(count, g):
                group_done(g)
                over_rms(head_a, acc[:, 0:2, 0:T]).then_inc(S["q_scaled"], 1)
                dve.wait_ge(S["q_scaled"], count)
                dve.sem_inc(acc_free[0])

            ahead(G_V, 1)
            dve.wait_ge(S["in_rms_in_psum"], 1)
            V.tensor_copy(in_rms[:], side[:, 2, 0:T]).then_inc(S["in_rms_ready"], 1)
            dve.wait_ge(S["in_rms_ready"], 1)
            scaled_heads(1, G_K)
            dve.wait_ge(S["param_cols_in_psum"], 1)
            V.tensor_copy(param_cols[:, BLOCKS:PARAMS], side[:, 0, BLOCKS:PARAMS])
            ahead(G_V, 2)
            dve.wait_ge(S["cache_k_in_psum"], 1)
            keys_by_half = keys_all.rearrange("p (t h) n -> p h t n", h=2)
            cached = side[:, 1, 0:D_KV].rearrange("p (t n) -> p t n", t=2)
            for half in range(2):
                for to in range(2):
                    last = V.tensor_copy(keys_by_half[64 * to:64 * to + 64, half, :, TP:TP + PAST],
                                         cached[64 * half:64 * half + 64])
            last.then_inc(S["param_cols_ready"], 1)
            dve.wait_ge(S["param_cols_ready"], 1)
            ahead(G_V, 3)
            ahead(G_MIX, 0)
            ahead(G_MIX, 1)
            rope(1, k_gain)
            group_done(G_V)
            over_rms(c_gate, acc[:, 2:4, 0:T]).then_inc(acc_free[1], 1)
            for half in range(2):
                for to in range(2):
                    src, dst = head_a[64 * half:64 * half + 64], keys_by_half[64 * to:64 * to + 64, half]
                    V.tensor_copy(dst[:, :, 0:TP], src[:, :, 0:TP])
                    last = V.tensor_copy(dst[:, :, TP + PAST:KEYS], src[:, :, TP:T])
            last.then_inc(S["keys_filled"], 1)
            ahead(G_MIX, 2)
            dve.wait_ge(S["v_in_psum"], 1)
            for t in range(2):
                rows = side[:, t, 0:2 * P].rearrange("p (b k d) -> p k b d", b=2, d=HEAD_DIM)
                V.tensor_copy(values_all[:, 2 * t:2 * t + 2, 0:2, :], rows)
            for t in range(2):
                rows = side[0:TS, t, 2 * P:3 * P].rearrange("p (k d) -> p k d", d=HEAD_DIM)
                last = V.tensor_copy(values_all[0:TS, 2 * t:2 * t + 2, 3, :], rows)
            last.then_inc(S["values_ready"], 1)
            dve.wait_ge(S["values_ready"], 1)
            dve.sem_inc(S["side_free"])

            PER_MIX = 18
            with dve.Fori(0, PAIRS) as j:
                own.begin_loop(j, PER_MIX)
                g = G_MIX + 4 * j
                ahead(g, 3)
                ahead(g + 1, 0)
                ahead(g + 1, 1)
                ahead(g + 1, 2)
                scaled_heads(j + 2, g)
                ahead(g + 1, 3)
                ahead(g + 2, 0)
                rope(j + 2, q_gain)
                for half in range(2):
                    r = slice(64 * half, 64 * half + 64)
                    last = V.tensor_copy(q_sample[r, half], head_a[r, :, TP:T])
                last.then_inc(S["q_sample_packed"], 1)
                ahead(g + 2, 1)
                ahead(g + 2, 2)
                group_done(g + 1)
                over_rms(c_gate, acc[:, 2:4, 0:T]).then_inc(acc_free[1], 1)
                dve.wait_ge(acc_free[1], 2 * j + 2)
                own.mark(over_rms(c_gate, c_gate))
                ahead(g + 2, 3)
                for u in range(4):
                    wait_apart(dve, S["scores_ready"], 5 * j + u + 1)
                    for half, lo, hi in ((0, 0, P), (1, P, 3 * P)):
                        c = 4 * half + u
                        last = V.tensor_tensor_reduce(
                            out=probs[:, u, lo:hi], in0=side[:, u, lo:hi], in1=mask[:, lo:hi], scale=SCALE,
                            scalar=sinks_cur[:, u:u + 1], op0=ALU.add, op1=ALU.max, accum_out=s_max[:, c:c + 1])
                    last.then_inc(S["scores_masked"], 1)
                dve.wait_ge(S["scores_masked"], 4 * j + 4)
                own.mark(V.tensor_scalar(s_neg, s_max, -1.0, None, ALU.mult))
                own.settle()
                V.tensor_tensor(s_sink[:, 0:4], s_neg[:, 0:4], sinks_cur[:, 0:4], ALU.add)
                V.tensor_tensor(s_sink[:, 4:8], s_neg[:, 4:8], sinks_cur[:, 0:4], ALU.add).then_inc(S["neg_max_ready"], 1)
                ahead(g + 3, 0)
                dve.wait_ge(S["scores_ready"], 5 * j + 5)
                own.mark(V.reduce_max(m_max, side[:, 0, 0:PAST + TS], AX_X))
                own.settle()
                own.mark(V.scalar_tensor_tensor(out=m_neg, in0=m_max, scalar=SCALE, in1=sinks_cur[:, 4:5],
                                                op0=ALU.mult, op1=ALU.max))
                own.settle()
                own.mark(V.tensor_scalar(m_neg, m_neg, -1.0, None, ALU.mult))
                own.settle()
                V.tensor_tensor(m_sink, m_neg, sinks_cur[:, 4:5], ALU.add).then_inc(S["neg_max_ready"], 1)
                ahead(g + 3, 1)
                ahead(g + 3, 2)
                group_done(g + 2)
                V.tensor_tensor(conv_in[:, :, 2:2 + TP], acc[:, 0:2, 0:TP], c_gate[:, :, 0:TP], ALU.mult)
                V.tensor_tensor(conv_in[:, :, TP + 4:UP], acc[:, 0:2, TP:T], c_gate[:, :, TP:T],
                                ALU.mult).then_inc(acc_free[0], 1)
                own.mark(V.tensor_copy(conv_in[:, :, TP + 2:TP + 4], state_cur[:].rearrange("p r t -> p t r")))
                own.settle()
                dve.wait_ge(acc_free[0], 2 * j + 3)
                tails = conv_tail[:].rearrange("p r (j t) -> p j t r", t=2)
                V.tensor_copy(tails[:, j, :, 0:2], conv_in[:, :, TP:TP + 2])
                V.tensor_copy(tails[:, j, :, 2:4], conv_in[:, :, UP - 2:UP])
                for w in range(3):
                    for t in range(2):
                        src, tap = conv_in[:, t, w:w + UP - 2], conv_w_cur[:, w, t:t + 1]
                        if w == 0:
                            own.mark(V.tensor_scalar(conv_y[:, t], src, tap, None, ALU.mult))
                        else:
                            own.mark(V.scalar_tensor_tensor(out=conv_y[:, t], in0=src, scalar=tap, in1=conv_y[:, t],
                                                            op0=ALU.mult, op1=ALU.add))
                    own.settle()
                V.tensor_tensor(conv_y[:, :, 0:TP], conv_y[:, :, 0:TP], wide(in_rms[:, 0:TP].unsqueeze(1), P, 2, TP),
                                ALU.mult)
                own.mark(V.tensor_tensor(conv_y[:, :, TP + 2:UP - 2], conv_y[:, :, TP + 2:UP - 2],
                                         wide(in_rms[:, TP:T].unsqueeze(1), P, 2, TS), ALU.mult))
                ahead(g + 3, 3)
                dve.wait_ge(S["probs_ready"], 2 * j + 2)
                V.tensor_tensor(s_inv, s_sum, s_sink, ALU.add)
                own.mark(V.tensor_tensor(m_inv, m_sum, m_sink, ALU.add))
                own.settle()
                V.reciprocal(s_inv, s_inv)
                own.mark(V.reciprocal(m_inv, m_inv))
                own.settle()
                ahead(g + 4, 0)
                ahead(g + 4, 1)
                dve.wait_ge(S["out_in_psum"], j + 1)
                V.tensor_tensor(out_heads[:].rearrange("p a u d -> p (a u) d"),
                                side[:, 1, :].rearrange("p (c d) -> p c d", d=HEAD_DIM),
                                wide(s_inv.unsqueeze(2), P, 8, HEAD_DIM), ALU.mult)
                V.tensor_scalar(out_sample[:], side[:, 3, 0:HEAD_DIM], m_inv, None, ALU.mult).then_inc(S["out_normed"], 1)
                ahead(g + 4, 2)
                group_done(g + 3)
                V.tensor_tensor(c_gate[:, :, 0:TP], acc[:, 2:4, 0:TP], conv_y[:, :, 0:TP], ALU.mult)
                V.tensor_tensor(c_gate[:, :, TP:T], acc[:, 2:4, TP:T], conv_y[:, :, TP + 2:UP - 2],
                                ALU.mult).then_inc(S["z_product_ready"], 1)
                dve.wait_ge(S["out_t_in_psum"], j + 1)
                for half in range(2):
                    last = V.tensor_copy(out_sample_t[64 * half:64 * half + 64],
                                         side[0:64, 2, 64 * half:64 * half + 64].rearrange("p (t n) -> p t n", t=2))
                last.then_inc(S["out_sample_copied"], 1)
                dve.wait_ge(S["z_hi_ready"], j + 1)
                V.tensor_tensor(z_lo_p[:, j], c_gate, z_hi_p[:, j].bitcast(F32), ALU.subtract).then_inc(acc_free[1], 1)
                dve.wait_ge(S["attn_hi_ready"], j + 1)
                V.tensor_tensor(at_lo_p[:, j, :, 0:TP], side[:, 0, :].rearrange("p (t n) -> p t n", t=2),
                                at_hi_p[:, j, :, 0:TP].bitcast(F32), ALU.subtract)
                V.tensor_tensor(at_lo_p[:, j, :, TP:T], out_sample_t[:], at_hi_p[:, j, :, TP:T].bitcast(F32),
                                ALU.subtract).then_inc(S["side_free"], 1)
                own.end_loop(PAIRS)

            def scaled_gate(count, g):
                group_done(g)
                over_rms(gate, acc[:, 0:2, 0:T]).then_inc(S["gate_scaled"], 1)
                dve.wait_ge(S["gate_scaled"], count)
                dve.sem_inc(acc_free[0])

            with dve.Fori(0, PAIRS) as j:
                g = G_ATT + 2 * j
                ahead(g, 3)
                ahead(g + 1, 0)
                ahead(g + 1, 1)
                ahead(g + 1, 2)
                scaled_gate(j + 1, g)
                ahead(g + 1, 3)
                ahead(g + 2, 0)
                ahead(g + 2, 1)
                ahead(g + 2, 2)
                group_done(g + 1)
                dve.wait_ge(S["gate_ready"], j + 1)
                V.tensor_tensor(gated_attn_p[:, j], acc[:, 2:4, 0:T], gate, ALU.mult).then_inc(acc_free[1], 1)
            with dve.Fori(0, PAIRS) as j:
                g = G_CONV + 2 * j
                ahead(g, 3)
                ahead(g + 1, 0)
                ahead(g + 1, 1)
                ahead(g + 1, 2)
                scaled_gate(j + PAIRS + 1, g)
                ahead(g + 1, 3)
                ahead(g + 2, 0)
                ahead(g + 2, 1)
                ahead(g + 2, 2)
                group_done(g + 1)
                dve.wait_ge(S["gate_ready"], j + PAIRS + 1)
                V.tensor_tensor(product, acc[:, 2:4, 0:T], gate, ALU.mult).then_inc(acc_free[1], 1)
                dve.wait_ge(acc_free[1], j + (G_CONV // 2 + 1))
                V.tensor_tensor(product, product, gated_attn_p[:, j], ALU.add).then_inc(S["product_ready"], 1)
                dve.wait_ge(S["merged_hi_ready"], j + 1)
                V.tensor_tensor(at_lo_p[:, j], product, at_hi_p[:, j].bitcast(F32), ALU.subtract
                                ).then_inc(S["merged_ready"], 1)

            dve.wait_ge(S["merged_ready"], PAIRS)
            own.mark(V.memset(square_sum, 0.0))
            ffn_gain = param_cols[:, BLOCKS:2 * BLOCKS].rearrange("p (j t o) -> p j t o", t=2, o=1)

            with dve.Fori(0, PAIRS // 2) as jj:
                own.begin_loop(jj, 2)
                for b in range(2):
                    j = 2 * jj + b
                    g = G_OUT + b + 2 * jj
                    ahead(g, 3)
                    ahead(g + 1, 0)
                    ahead(g + 1, 1)
                    ahead(g + 1, 2)
                    group_done(g)
                    dve.wait_ge(S["x_res_copied"], j + 1)
                    V.tensor_tensor(residual_p[:, j], residual_p[:, j], acc[:, 2 * b:2 * b + 2, 0:T],
                                    ALU.add).then_inc(S["residual_ready"], 1)
                    dve.wait_ge(S["residual_ready"], j + 1)
                    dve.sem_inc(acc_free[b])
                    dve.wait_ge(S["squared"], j + 1)
                    own.settle()
                    own.mark(V.tensor_tensor(square_sum, square_sum, squares, ALU.add))
                    dve.wait_ge(S["ffn_hi_ready"], j + 1)
                    for t in range(2):
                        last = V.scalar_tensor_tensor(out=xn_lo_p[:, j, t], in0=residual_p[:, j, t],
                                                      scalar=ffn_gain[:, j, t], in1=xn_hi_p[:, j, t].bitcast(F32),
                                                      op0=ALU.mult, op1=ALU.subtract)
                    last.then_inc(S["ffn_in_ready"], 1)
                own.end_loop(PAIRS // 2)
            own.settle()
            dve.sem_inc(S["square_sum_ready"])
            dve.wait_ge(S["ffn_rms_ready"], 1)
            own.mark(V.reciprocal(inv_rms, inv_rms))
            own.settle()
            over_rms_ffn = wide(inv_rms.unsqueeze(1), P, 2, T)

            done_pairs = 0
            for part, (cols, _) in enumerate(FFN_PARTS):
                with dve.Fori(0, cols) as i:
                    g = G_FFN[part] + 2 * i
                    own.begin_loop(i, 1)
                    ahead(g, 3)
                    ahead(g + 1, 0)
                    ahead(g + 1, 1)
                    ahead(g + 1, 2)
                    group_done(g)
                    V.tensor_tensor(silu, acc[:, 0:2, 0:T], over_rms_ffn, ALU.mult).then_inc(S["gate_product_ready"], 1)
                    dve.wait_ge(S["gate_product_ready"], done_pairs + i + 1)
                    dve.sem_inc(acc_free[0])
                    ahead(g + 1, 3)
                    ahead(g + 2, 0)
                    dve.wait_ge(S["silu_ready"], done_pairs + i + 1)
                    own.mark(V.tensor_tensor(silu, silu, over_rms_ffn, ALU.mult))
                    ahead(g + 2, 1)
                    ahead(g + 2, 2)
                    group_done(g + 1)
                    own.settle()
                    V.tensor_tensor(hidden, acc[:, 2:4, 0:T], silu, ALU.mult).then_inc(S["hidden_product_ready"], 1)
                    dve.wait_ge(S["hidden_hi_ready"], done_pairs + i + 1)
                    V.tensor_tensor(at_lo_p[:, i], hidden, at_hi_p[:, i].bitcast(F32), ALU.subtract
                                    ).then_inc(acc_free[1], 1)
                    own.end_loop(cols)
                done_pairs += cols
                g_down = G_FFN[part] + 2 * cols
                if part < len(FFN_PARTS) - 1:
                    with dve.Fori(0, PAIRS // 2) as jj:
                        for b in range(2):
                            g = g_down + b + 2 * jj
                            ahead(g, 3)
                            ahead(g + 1, 0)
                            ahead(g + 1, 1)
                            ahead(g + 1, 2)
                            group_done(g)
                            if part:
                                dve.wait_ge(acc_free[b], (G_FFN[part - 1] + 2 * FFN_PARTS[part - 1][0] + b) // 2 + 1 + jj)
                            V.tensor_tensor(residual_p[:, 2 * jj + b], residual_p[:, 2 * jj + b],
                                            acc[:, 2 * b:2 * b + 2, 0:T], ALU.add).then_inc(acc_free[b], 1)

            def add_last(j, jj, b):
                group_done(g_down + b + 2 * jj)
                dve.wait_ge(acc_free[b], (G_FFN[part - 1] + 2 * FFN_PARTS[part - 1][0] + b) // 2 + 1 + jj)
                if not (isinstance(j, int) and j == 0):
                    dve.wait_ge(S["y_in_psum"], j)
                V.tensor_tensor(y_cols, residual_p[:, j], acc[:, 2 * b:2 * b + 2, 0:T], ALU.add).then_inc(S["y_ready"], 1)
                dve.wait_ge(S["y_ready"], j + 1)
                dve.sem_inc(acc_free[b])

            def last_group(j, jj, b):
                g = g_down + b + 2 * jj
                ahead(g, 3)
                ahead(g + 1, 0)
                ahead(g + 1, 1)
                ahead(g + 1, 2)
                add_last(j, jj, b)

            last_group(0, 0, 0)
            last_group(1, 0, 1)
            with dve.Fori(1, PAIRS // 2 - 1) as jj:
                last_group(2 * jj, jj, 0)
                last_group(2 * jj + 1, jj, 1)
            last_group(PAIRS - 2, PAIRS // 2 - 1, 0)
            ahead(g_down + PAIRS - 1, 3)
            add_last(PAIRS - 1, PAIRS // 2 - 1, 1)

        @block.tensor
        def _(pe):
            T_ = nc.tensor

            def piece(g, s, pair, hi, lo, blocks=4, each=None):
                pe.wait_ge(S["lo_ready"], 4 * g + s + 1)
                for m in range(2):
                    out = acc[:, pair + m, 0:T]
                    cols = slice(m * P, (m + 1) * P)
                    for k in range(blocks):
                        b = blocks * s + k
                        first, end = s == 0 and k == 0, s == SLOTS - 1 and k == blocks - 1
                        T_.matmul(out, w_hi[:, s, k, cols], hi[:, b], start=first, stop=False)
                        T_.matmul(out, w_hi[:, s, k, cols], lo[:, b], start=False, stop=False)
                        last = T_.matmul(out, w_lo[:, s, k, cols], hi[:, b], start=False, stop=end)
                last.then_inc(S["piece_done"], 1)

            def turn(pair, count):
                pe.wait_ge(acc_free[pair // 2], count)

            def transpose_quarter(s):
                pe.wait_ge(x_loaded[s], 32)
                for k in range(4 * s, 4 * s + 4):
                    if k >= 4:
                        pe.wait_ge(S["xn_ready"], k - 3)
                    for n, rows in enumerate(x_rows):
                        r = rows.shape[0]
                        last = T_.transpose(side[:, k % 4, n * P:n * P + r], rows[:, k * P:(k + 1) * P], ident[0:r, 0:r])
                    last.then_inc(S["x_transposed"], 1)

            def sum_squares(count):
                pe.wait_ge(S["q_squared"], count)
                for t in range(2):
                    last = T_.matmul(side[:, t, 0:T], same_head, head_b[:, t], start=True, stop=True)
                last.then_inc(S["ssq_ready"], 1)

            pe.wait_ge(S["first_consts_loaded"], 16)
            pe.wait_ge(S["first_params_loaded"], 16)
            T_.transpose(acc[:, 3, 0:BLOCKS], params[0:BLOCKS, :], ident[0:BLOCKS, 0:BLOCKS]).then_inc(S["gain_in_psum"], 1)
            transpose_quarter(0)
            for s in range(SLOTS):
                if s + 1 < SLOTS:
                    transpose_quarter(s + 1)
                pe.wait_ge(S["xn_ready"], 4 * s + 4)
                piece(G_K, s, 0, xn_hi, xn_lo)
            pe.wait_ge(S["params_loaded"], 16 * 7)
            T_.transpose(side[:, 0, 0:PARAMS], params[0:PARAMS, :], ident[0:PARAMS, 0:PARAMS]
                         ).then_inc(S["param_cols_in_psum"], 1)
            pe.wait_ge(S["cache_k_loaded"], 16)
            for t in range(2):
                last = T_.transpose(side[:, 1, t * P:(t + 1) * P], cache_k_rows[:, t * P:(t + 1) * P], ident)
            last.then_inc(S["cache_k_in_psum"], 1)
            pe.wait_ge(S["consts_loaded"], 16)
            for s in range(SLOTS):
                piece(G_V, s, 2, xn_hi, xn_lo)
                if s == 0:
                    pe.wait_ge(S["diagonal_ready"], 1)
                    for n, r in enumerate((P, P, TS)):
                        last = T_.matmul(side[:, 2, n * P:n * P + r], ones[0:r, :], diagonals[n][0:r, 0:r],
                                         start=True, stop=True)
                    last.then_inc(S["in_rms_in_psum"], 1)
                if s == 1:
                    pe.wait_ge(S["param_cols_ready"], 1)
                    sum_squares(1)

            def key_value_rows():
                pe.wait_ge(S["q_roped"], 1)
                for t in range(2):
                    T_.transpose(side[:, 2, t * P:(t + 1) * P], head_a[:, t, P:2 * P], ident)
                    last = T_.transpose(side[0:TS, 3, t * P:(t + 1) * P], head_a[:, t, TP:T], ident)
                last.then_inc(S["k_rows_in_psum"], 1)
                pe.wait_ge(acc_free[1], 1)
                for t in range(2):
                    for n in range(2):
                        T_.transpose(side[:, t, n * P:(n + 1) * P], c_gate[:, t, n * P:(n + 1) * P], ident)
                    last = T_.transpose(side[0:TS, t, 2 * P:3 * P], c_gate[:, t, TP:T], ident)
                last.then_inc(S["v_in_psum"], 1)

            def transpose_probs(u, bank):
                for n in range(3):
                    last = T_.transpose(side[:, bank, n * P:(n + 1) * P], probs[:, u, n * P:(n + 1) * P], ident)
                last.then_inc(S["probs_in_psum"], 1)

            def head_out(u):
                t = probs_t[:, u % 2]
                o = u * HEAD_DIM
                T_.matmul(side[:, 1, o:o + HEAD_DIM], t[:, 0:P], values_cur[:, 0], start=True, stop=True)
                o += 4 * HEAD_DIM
                T_.matmul(side[:, 1, o:o + HEAD_DIM], t[:, P:2 * P], values_cur[:, 0], start=True, stop=False)
                return T_.matmul(side[:, 1, o:o + HEAD_DIM], t[:, 2 * P:3 * P], values_cur[:, 1], start=False, stop=True)

            def mix(j, first=False):
                g = G_MIX + 4 * j
                turn(0, 2 * j + 1)
                for s in range(SLOTS):
                    piece(g, s, 0, xn_hi, xn_lo)
                    if first and s == 0:
                        key_value_rows()
                turn(2, 2 * j + 1)
                for s in range(SLOTS):
                    piece(g + 1, s, 2, xn_hi, xn_lo)
                    if s == 0:
                        pe.wait_ge(S["side_free"], j + 1)
                        sum_squares(j + 2)
                turn(0, 2 * j + 2)
                for s in range(SLOTS):
                    piece(g + 2, s, 0, xn_hi, xn_lo)
                    if s == 0:
                        pe.wait_ge(S["kv_staged"], j + 1)
                        pe.wait_ge(S["q_roped"], j + 2)
                        for u in range(4):
                            t, r = u // 2, slice(64 * (u % 2), 64 * (u % 2) + 64)
                            T_.matmul(side[:, u, 0:P], head_a[r, t, 0:P], keys_cur[r, 0:P], start=True, stop=True)
                            T_.matmul(side[:, u, P:3 * P], head_a[r, t, P:2 * P], keys_cur[r, 0:TP],
                                      start=True, stop=True).then_inc(S["scores_ready"], 1)
                    if s == 1:
                        pe.wait_ge(S["scores_masked"], 4 * j + 1)
                        pe.wait_ge(S["q_sample_packed"], j + 1)
                        T_.matmul(side[:, 0, 0:PAST + TS], q_sample[:].rearrange("p h t n -> p (h t n)"),
                                  keys_cur[:, TP:KEYS], start=True, stop=True).then_inc(S["scores_ready"], 1)
                    if s == 3:
                        pe.wait_ge(S["probs_ready"], 2 * j + 1)
                        transpose_probs(0, 1)
                        transpose_probs(1, 2)
                turn(2, 2 * j + 2)
                for s in range(SLOTS):
                    piece(g + 3, s, 2, xn_hi, xn_lo)
                    if s == 0:
                        pe.wait_ge(S["probs_copied"], 5 * j + 2)
                        head_out(0)
                        head_out(1)
                        transpose_probs(2, 3)
                        pe.wait_ge(S["probs_ready"], 2 * j + 2)
                        transpose_probs(3, 0)
                    if s == 1:
                        T_.transpose(side[:, 2, 0:P], probs_sample[:, 0:P], ident)
                        T_.transpose(side[0:TS, 2, P:2 * P], probs_sample[:, P:P + TS], ident
                                     ).then_inc(S["probs_in_psum"], 1)
                    if s == 2:
                        pe.wait_ge(S["probs_copied"], 5 * j + 5)
                        head_out(2)
                        head_out(3)
                        T_.matmul(side[:, 3, 0:HEAD_DIM], probs_t_sample[:, 0], values_cur[:, 2], start=True, stop=False)
                        T_.matmul(side[:, 3, 0:HEAD_DIM], probs_t_sample[0:TS, 1], values_cur[0:TS, 3], start=False,
                                  stop=True).then_inc(S["out_in_psum"], 1)
                pe.wait_ge(S["out_normed"], j + 1)
                for t in range(2):
                    for n in range(2):
                        c = t * 2 * P + n * P
                        T_.transpose(side[:, 0, c:c + P], out_heads[:, n, 2 * t:2 * t + 2, :].rearrange("p u d -> p (u d)"),
                                     ident)
                T_.transpose(side[0:HEAD_DIM, 2, 0:P], out_sample[:], ident).then_inc(S["out_t_in_psum"], 1)

            mix(0, first=True)
            with pe.Fori(1, PAIRS) as j:
                mix(j)

            for first, hi, lo in ((G_ATT, at_hi, at_lo), (G_CONV, z_hi, z_lo)):
                with pe.Fori(0, PAIRS) as j:
                    g = first + 2 * j
                    turn(0, j + first // 2)
                    for s in range(SLOTS):
                        piece(g, s, 0, xn_hi, xn_lo)
                    turn(2, j + first // 2)
                    if first == G_ATT:
                        pe.wait_ge(S["side_free"], PAIRS + 1)
                    for s in range(SLOTS):
                        piece(g + 1, s, 2, hi, lo)

            pe.wait_ge(S["side_free"], PAIRS + 1)
            T_.transpose(side[0:4 * BLOCKS, 2, 0:P], conv_tail[:].rearrange("p r b -> p (r b)"), ident
                         ).then_inc(S["tails_in_psum"], 1)
            with pe.Fori(0, PAIRS // 2) as jj:
                for b in range(2):
                    j = 2 * jj + b
                    turn(2 * b, jj + G_OUT // 2)
                    for s in range(SLOTS):
                        pe.wait_ge(S["merged_ready"], 2 * s + 2)
                        piece(G_OUT + b + 2 * jj, s, 2 * b, at_hi, at_lo)
                        if s == 2:
                            pe.wait_ge(S["x_res_loaded"], 32 * j + 32)
                            for t in range(2):
                                for n in range(2):
                                    c = t * 2 * P + n * P
                                    T_.transpose(side[:, 0, c:c + P], x_res[:, n, t * P:(t + 1) * P], ident)
                                last = T_.transpose(side[:, 1, t * TS:(t + 1) * TS], x_res[0:TS, 2, t * P:(t + 1) * P],
                                                    ident[0:TS, 0:TS])
                            last.then_inc(S["x_res_in_psum"], 1)
            def mean_square():
                pe.wait_ge(S["square_sum_ready"], 1)
                for t in range(2):
                    last = T_.matmul(side[:, 3, 0:T], ones, square_sum[:, t], start=t == 0, stop=t == 1)
                last.then_inc(S["mean_in_psum"], 1)

            for part, (cols, blocks) in enumerate(FFN_PARTS):
                g = G_FFN[part]

                def gate_up(i, g, first=False):
                    turn(0, i + G_FFN[part] // 2)
                    for s in range(SLOTS):
                        if first:
                            pe.wait_ge(S["ffn_in_ready"], 2 * s + 2)
                        piece(g, s, 0, xn_hi, xn_lo)
                        if first and s == 0:
                            mean_square()
                    turn(2, i + G_FFN[part] // 2)
                    for s in range(SLOTS):
                        piece(g + 1, s, 2, xn_hi, xn_lo)

                if part == 0:
                    gate_up(0, g, first=True)
                with pe.Fori(1 if part == 0 else 0, cols) as i:
                    gate_up(i, g + 2 * i)
                g_down = g + 2 * cols

                def down(b, jj):
                    turn(2 * b, g_down // 2 + jj)
                    for s in range(SLOTS):
                        if b == 0 and s == SLOTS - 1:
                            turn(2, g_down // 2)
                        piece(g_down + b + 2 * jj, s, 2 * b, at_hi, at_lo, blocks)

                if part < len(FFN_PARTS) - 1:
                    with pe.Fori(0, PAIRS // 2) as jj:
                        for b in range(2):
                            down(b, jj)

            def transpose_y(j):
                pe.wait_ge(S["y_ready"], j + 1)
                if not (isinstance(j, int) and j == 0):
                    pe.wait_ge(S["y_rows_ready"], j)
                for t in range(2):
                    for n in range(2):
                        T_.transpose(side[:, 0, n * GROUP_COLS + t * P:n * GROUP_COLS + (t + 1) * P],
                                     y_cols[:, t, n * P:(n + 1) * P], ident)
                    last = T_.transpose(side[0:TS, 1, t * P:(t + 1) * P], y_cols[:, t, TP:T], ident)
                last.then_inc(S["y_in_psum"], 1)

            def last_down(b, jj, j):
                turn(2 * b, g_down // 2 + jj)
                for s in range(SLOTS):
                    if j is None and s == SLOTS - 1:
                        turn(2, g_down // 2)
                    piece(g_down + b + 2 * jj, s, 2 * b, at_hi, at_lo, blocks)
                    if s == 1 and j is not None:
                        transpose_y(j)

            last_down(0, 0, None)
            last_down(1, 0, 0)
            with pe.Fori(1, PAIRS // 2) as jj:
                last_down(0, jj, 2 * jj - 1)
                last_down(1, jj, 2 * jj)
            transpose_y(PAIRS - 1)


def constant_columns(frames, sample_frames, past):
    half = HEAD_DIM // 2
    pos = np.concatenate([np.arange(frames), past + np.arange(sample_frames)]).astype(np.float32)
    inv = np.exp(np.float32(-np.log(ROPE_THETA)) * np.arange(half, dtype=np.float32) * np.float32(2.0 / HEAD_DIM))
    ang = (inv[:, None] * pos[None, :]).astype(np.float32)
    cos, sin = np.cos(ang), np.sin(ang)
    heads = P // HEAD_DIM
    rows = np.arange(P)
    mask = np.zeros((P, 3 * P), np.float32)
    mask[:CHUNK, CHUNK:P] = NEG_INF
    mask[:CHUNK, P + 3 * CHUNK:] = NEG_INF
    mask[CHUNK:, P:P + CHUNK] = NEG_INF
    return np.concatenate([
        np.eye(P), np.ones((P, P)), np.full((P, 1), EPS), np.tile(cos, (2 * heads, 1)),
        np.tile(np.concatenate([sin, -sin]), (heads, 1)), rows[:, None] // HEAD_DIM == rows[None, :] // HEAD_DIM, mask,
    ], axis=1).astype(np.float32)


INPUTS = ["x_prompt", "x_sample", "cache_k", "cache_v", "state_conv", "norm_mix_g", "w_in", "q_norm_g",
          "k_norm_g", "attn_sinks", "conv_w", "w_attn_proj", "w_conv_proj", "w_out", "norm_ffn_g",
          "w_ffn_gate", "w_ffn_up", "w_ffn_down"]


def kernel(**inputs):
    import concourse.bacc as bacc
    from concourse.bass_utils import run_bass_kernel_spmd

    nc = bacc.Bacc("TRN2", target_bir_lowering=False, num_devices=1)
    xp, xs, ck = inputs["x_prompt"].shape, inputs["x_sample"].shape, inputs["cache_k"].shape
    arrays, args = {}, []
    data = {n: np.ascontiguousarray(inputs[n]) for n in INPUTS}
    data["constants"] = constant_columns(xp[1], xs[1], ck[2])
    for name, a in data.items():
        arrays[f"in_{name}"] = a
        args.append(nc.dram_tensor(f"in_{name}", a.shape, mybir.dt.from_np(a.dtype), kind="ExternalInput").ap())
    depth, kv = ck[0], ck[3:]
    window = min(128, xp[1])
    conv = inputs["state_conv"].shape
    shapes = [xp, xs, (depth, xp[0], window) + kv, (depth, xp[0], window) + kv, (depth, xp[0]) + conv[2:],
              (depth, xs[0], xs[1]) + kv, (depth, xs[0], xs[1]) + kv, conv]
    for i, shape in enumerate(shapes):
        args.append(nc.dram_tensor(f"out_{i}", tuple(shape), F32, kind="ExternalOutput").ap())
    encoder_layer(nc, *args)
    r = run_bass_kernel_spmd(nc, [arrays], core_ids=[0])
    return tuple(r.results[0][f"out_{i}"] for i in range(len(shapes)))
```
